# Optimizing a Trainium2 kernel written in Bass

```python
import jax, jax.numpy as jnp
from jax import lax
import numpy as np

D_MODEL = 1024
BATCH = 1
SEQ = 1024
DEPTH = 2
DEC_BATCH = 8
DEC_SEQ = 4
PAST_LEN = 512
PAGE_SIZE = 128

N_MIXERS = 2
N_A_LAYERS = (DEPTH + 1) // 2
N_B_LAYERS = DEPTH // 2
N_HEADS = 8
HEAD_DIM = D_MODEL // N_HEADS
N_KV_HEADS = 2
GROUP = N_HEADS // N_KV_HEADS
IDX_HEADS = 8
IDX_DIM = 64
TOPK_MAX = 256
Q_BLOCK = 128
POOL_WINDOWS = (2, 4, 8, 16)
N_POOL_GROUPS = len(POOL_WINDOWS)
POOL_GROUP_DIM = D_MODEL // N_POOL_GROUPS
POOL_STATE = max(POOL_WINDOWS) - 1
D_FF = 4 * D_MODEL
RMS_EPS = 1e-6
Q_W = N_HEADS * HEAD_DIM
KV_W = N_KV_HEADS * HEAD_DIM
QI_W = IDX_HEADS * IDX_DIM
PROJ_SPLITS = (Q_W, Q_W + KV_W, Q_W + 2 * KV_W, Q_W + 2 * KV_W + QI_W, Q_W + 2 * KV_W + QI_W + IDX_DIM)
D_PROJ = Q_W + 2 * KV_W + QI_W + IDX_DIM + IDX_HEADS

kernel_name = 'dsa_pool_hybrid_step'

def rmsnorm(x, g):
    xf = x.astype(jnp.float32)
    y = xf * lax.rsqrt(jnp.mean(xf * xf, axis=-1, keepdims=True) + RMS_EPS)
    return (y * g.astype(jnp.float32)).astype(x.dtype)

def modulate(h, shift, scale):
    return h * (1 + scale[:, None, :]) + shift[:, None, :]

def dsa_block(qb, qib, wib, posb, keys, vals, kidx, k_sel):
    n, qblk = qb.shape[0], qb.shape[1]
    L = keys.shape[1]
    logits = jnp.einsum('nqhd,nsd->nqhs', qib.astype(jnp.float32), kidx.astype(jnp.float32)) * (IDX_DIM ** -0.5)
    score = jnp.einsum('nqhs,nqh->nqs', jax.nn.relu(logits), wib.astype(jnp.float32)) * (IDX_HEADS ** -0.5)
    causal = jnp.arange(L)[None, :] <= posb[:, None]
    score = jnp.where(causal[None], score, -jnp.inf)
    _, idx = lax.top_k(score, k_sel)
    valid = idx <= posb[None, :, None]
    k_g = jax.vmap(lambda a, i: a[i])(keys, idx)
    v_g = jax.vmap(lambda a, i: a[i])(vals, idx)
    s = jnp.einsum('nqgrd,nqkgd->nqgrk', qb.astype(jnp.float32), k_g.astype(jnp.float32)) * (HEAD_DIM ** -0.5)
    s = jnp.where(valid[:, :, None, None, :], s, -jnp.inf)
    p = jax.nn.softmax(s, axis=-1)
    o = jnp.einsum('nqgrk,nqkgd->nqgrd', p, v_g.astype(jnp.float32))
    return o.reshape(n, qblk, N_HEADS * HEAD_DIM).astype(qb.dtype)

def dsa_mixer(h, w_in, w_o, past_k, past_v, past_kidx, pos0):
    n, t, _ = h.shape
    proj = h @ w_in
    q, k, v, qi, ki, wi = jnp.split(proj, PROJ_SPLITS, axis=-1)
    q = q.reshape(n, t, N_KV_HEADS, GROUP, HEAD_DIM)
    k = k.reshape(n, t, N_KV_HEADS, HEAD_DIM)
    v = v.reshape(n, t, N_KV_HEADS, HEAD_DIM)
    qi = qi.reshape(n, t, IDX_HEADS, IDX_DIM)
    if past_k is None:
        keys, vals, kidx = k, v, ki
    else:
        keys = jnp.concatenate([past_k.astype(k.dtype), k], axis=1)
        vals = jnp.concatenate([past_v.astype(v.dtype), v], axis=1)
        kidx = jnp.concatenate([past_kidx.astype(ki.dtype), ki], axis=1)
    L = keys.shape[1]
    k_sel = min(TOPK_MAX, L // 4)
    qb = min(Q_BLOCK, t)
    nblk = t // qb

    def to_blocks(a):
        return jnp.moveaxis(a.reshape((n, nblk, qb) + a.shape[2:]), 1, 0)

    pos = pos0 + jnp.arange(t)
    xs = (to_blocks(q), to_blocks(qi), to_blocks(wi), pos.reshape(nblk, qb))
    o = lax.map(lambda a: dsa_block(a[0], a[1], a[2], a[3], keys, vals, kidx, k_sel), xs)
    o = jnp.moveaxis(o, 0, 1).reshape(n, t, N_HEADS * HEAD_DIM)
    return o @ w_o, (k, v, ki)

def pool_mixer(h, prev, pos0, w_grp, scale):
    n, t, d = h.shape
    ext = jnp.concatenate([prev.astype(h.dtype), h], axis=1)
    cs = jnp.pad(jnp.cumsum(ext.astype(jnp.float32), axis=1), ((0, 0), (1, 0), (0, 0)))
    P = POOL_STATE
    end = cs[:, P + 1:P + 1 + t]
    pos = pos0 + jnp.arange(t)
    parts = []
    for g, w in enumerate(POOL_WINDOWS):
        lo, hi = g * POOL_GROUP_DIM, (g + 1) * POOL_GROUP_DIM
        win = end[..., lo:hi] - cs[:, P + 1 - w:P + 1 - w + t, lo:hi]
        cnt = jnp.minimum(w, pos + 1).astype(jnp.float32)[None, :, None]
        parts.append(win / cnt - h[..., lo:hi].astype(jnp.float32))
    pooled = jnp.stack(parts, axis=2)
    out = jnp.einsum('ntgc,gcd->ntgd', pooled, w_grp.astype(jnp.float32)).reshape(n, t, d)
    out = out * scale.astype(jnp.float32)
    return out.astype(h.dtype), ext[:, -P:]

def sq_relu_mlp(h, w_up, w_down):
    return jnp.square(jax.nn.relu(h @ w_up)) @ w_down

def setup_inputs(seed: int = 0) -> dict:
    key = jax.random.key(seed)
    ks = jax.random.split(key, 24)
    f32 = jnp.float32
    n_pages = PAST_LEN // PAGE_SIZE
    n_used = DEC_BATCH * n_pages
    n_pool = n_used + n_used // 4

    def nrm(k, shape, s):
        return jax.random.normal(k, shape, f32) * s

    page_table = jax.random.permutation(ks[6], n_pool)[:n_used].reshape(DEC_BATCH, n_pages).astype(jnp.int32)
    return {
        'x_prompt': nrm(ks[0], (BATCH, SEQ, D_MODEL), 1.0),
        'x_sample': nrm(ks[1], (DEC_BATCH, DEC_SEQ, D_MODEL), 1.0),
        'cache_k': nrm(ks[2], (N_A_LAYERS, n_pool, PAGE_SIZE, N_KV_HEADS, HEAD_DIM), 1.0),
        'cache_v': nrm(ks[3], (N_A_LAYERS, n_pool, PAGE_SIZE, N_KV_HEADS, HEAD_DIM), 1.0),
        'cache_kidx': nrm(ks[4], (N_A_LAYERS, n_pool, PAGE_SIZE, IDX_DIM), 1.0),
        'state_pool': nrm(ks[5], (N_B_LAYERS, DEC_BATCH, POOL_STATE, D_MODEL), 1.0),
        'page_table': page_table,
        'c_prompt': nrm(ks[7], (BATCH, D_MODEL), 1.0),
        'c_sample': nrm(ks[8], (DEC_BATCH, D_MODEL), 1.0),
        'norm_mix_g': 1.0 + nrm(ks[9], (DEPTH, D_MODEL), 0.05),
        'norm_ffn_g': 1.0 + nrm(ks[10], (DEPTH, D_MODEL), 0.05),
        'w_mod': nrm(ks[11], (DEPTH, D_MODEL, 6 * D_MODEL), 0.5 * D_MODEL ** -0.5),
        'b_mod': nrm(ks[12], (DEPTH, 6 * D_MODEL), 0.02),
        'dsa_w_in': nrm(ks[13], (N_A_LAYERS, D_MODEL, D_PROJ), D_MODEL ** -0.5),
        'dsa_w_o': nrm(ks[14], (N_A_LAYERS, N_HEADS * HEAD_DIM, D_MODEL), (N_HEADS * HEAD_DIM) ** -0.5),
        'pool_w': nrm(ks[15], (N_B_LAYERS, N_POOL_GROUPS, POOL_GROUP_DIM, POOL_GROUP_DIM), POOL_GROUP_DIM ** -0.5),
        'pool_scale': 1.0 + nrm(ks[16], (N_B_LAYERS, D_MODEL), 0.1),
        'w_up': nrm(ks[17], (DEPTH, D_MODEL, D_FF), D_MODEL ** -0.5),
        'w_down': nrm(ks[18], (DEPTH, D_FF, D_MODEL), D_FF ** -0.5),
        'final_norm_g': 1.0 + nrm(ks[19], (D_MODEL,), 0.05),
    }

def reference(x_prompt, x_sample, cache_k, cache_v, cache_kidx, state_pool, page_table, c_prompt, c_sample,
              norm_mix_g, norm_ffn_g, w_mod, b_mod, dsa_w_in, dsa_w_o, pool_w, pool_scale, w_up, w_down,
              final_norm_g):
    def run(x, c, is_sample):
        n = x.shape[0]
        pos0 = PAST_LEN if is_sample else 0
        mod_in = jax.nn.silu(c)
        new_k, new_v, new_ki, new_pool = [], [], [], []
        for i in range(DEPTH):
            mod = mod_in @ w_mod[i] + b_mod[i]
            sh1, sc1, g1, sh2, sc2, g2 = jnp.split(mod, 6, axis=-1)
            h = modulate(rmsnorm(x, norm_mix_g[i]), sh1, sc1)
            j = i // N_MIXERS
            if i % N_MIXERS == 0:
                if is_sample:
                    pk = cache_k[j][page_table].reshape(n, -1, N_KV_HEADS, HEAD_DIM)
                    pv = cache_v[j][page_table].reshape(n, -1, N_KV_HEADS, HEAD_DIM)
                    pki = cache_kidx[j][page_table].reshape(n, -1, IDX_DIM)
                else:
                    pk, pv, pki = None, None, None
                m, (k_rows, v_rows, ki_rows) = dsa_mixer(h, dsa_w_in[j], dsa_w_o[j], pk, pv, pki, pos0)
                new_k.append(k_rows)
                new_v.append(v_rows)
                new_ki.append(ki_rows)
            else:
                prev = state_pool[j] if is_sample else jnp.zeros((n, POOL_STATE, D_MODEL), h.dtype)
                m, st = pool_mixer(h, prev, pos0, pool_w[j], pool_scale[j])
                new_pool.append(st)
            x = x + g1[:, None, :] * m
            h = modulate(rmsnorm(x, norm_ffn_g[i]), sh2, sc2)
            x = x + g2[:, None, :] * sq_relu_mlp(h, w_up[i], w_down[i])
        y = rmsnorm(x, final_norm_g)
        return y, jnp.stack(new_k), jnp.stack(new_v), jnp.stack(new_ki), jnp.stack(new_pool)

    y_prompt, k_p, v_p, ki_p, pool_p = run(x_prompt, c_prompt, False)
    y_sample, k_s, v_s, ki_s, pool_s = run(x_sample, c_sample, True)
    return (y_prompt, y_sample, k_p, v_p, ki_p, pool_p, k_s, v_s, ki_s, pool_s)


_drawn_inputs = setup_inputs


def setup_inputs(seed=0):
    import zlib

    import numpy as np

    out = dict(_drawn_inputs(seed))
    spreads = {}
    factors = {}
    for name, (base, spread) in spreads.items():
        noise = np.random.default_rng([zlib.crc32(name.encode()), seed]).standard_normal(out[name].shape)
        drawn = base * np.exp(spread * noise) if base else spread * noise
        out[name] = __import__('jax').numpy.asarray(drawn.astype(out[name].dtype))
    for name, factor in factors.items():
        out[name] = (out[name] * factor).astype(out[name].dtype)
    return out
```

```python
from contextlib import ExitStack

import numpy as np

import concourse.bass as bass
from concourse import mybir

ALU = mybir.AluOpType
ACT = mybir.ActivationFunctionType
F32 = mybir.dt.float32
F32R = mybir.dt.float32r
I32 = mybir.dt.int32

D = 1024
SEQ = 1024
NB = 8
DT = 4
PAST = 512
PAGE = 128
PAGES = PAST // PAGE
HEADS = 8
HD = 128
KV = 2
GROUP = HEADS // KV
IH = 8
ID = 64
TOPK = 256
PS = 15
FF = 4 * D
QW, KW, IW = HEADS * HD, KV * HD, IH * ID
EPS = 1e-6

P = 128
KT8 = D // P
NS = NB * DT
ROWS = SEQ + NS
NC = 3
CW = ROWS // NC
LASTP = SEQ - 2 * CW
TILES = SEQ // P
NVEC = 6 * KT8
UNIT = KT8 * P
SL = PAST + DT
SAMPLE_K = min(TOPK, SL // 4)
SC_ATT = HD ** -0.5
SC_IDX = ID ** -0.5

NEG = -1.0e30
DECOY = -2.0e38
TAKEN = -3.0e38
CUT = -2.5e38

FB = 8
U_IN, N_IN = 0, 18
U_O = U_IN + N_IN
U_MLP0 = U_O + 8
U_POOL = U_MLP0 + 8 * FB
U_MLP1 = U_POOL + 2
G_IN = 0
G_O = G_IN + 3 * N_IN
G_MLP0 = G_O + 24
G_POOL = G_MLP0 + 24 * FB
G_MLP1 = G_POOL + 24

C_ID, C_CM, C_ONE, C_EH, C_SEL, C_RB, C_CMS, C_INV = 0, 128, 256, 384, 512, 576, 832, 836
C_ALL = C_INV + 64


def constants():
    c = np.zeros((P, C_ALL), np.float32)
    i = np.arange(P)
    c[:, C_ID:C_ID + P] = np.eye(P)
    c[:, C_CM:C_CM + P] = np.where(i[None, :] <= i[:, None], 0.0, NEG)
    c[:, C_ONE:C_ONE + P] = 1.0 / D
    j, h, t = i // 32, (i % 32) // DT, i % DT
    c[0:IH, C_EH:C_EH + P] = np.arange(IH)[:, None] == h[None, :]
    b, u = np.arange(NS) // DT, np.arange(NS) % DT
    for g in range(2):
        same = (b[None, :] == (j + 4 * g)[:, None]) & (u[None, :] == t[:, None])
        c[:, C_SEL + 32 * g:C_SEL + 32 * g + 32] = same
        c[0:NS, C_RB + 128 * g:C_RB + 128 * g + 128] = same.T
    c[0:NS, C_CMS:C_CMS + DT] = np.where(np.arange(DT)[None, :] <= u[:, None], 0.0, NEG)
    for g in range(4):
        c[:, C_INV + 16 * g:C_INV + 16 * g + 16] = 1.0 / np.minimum(2 << g, np.arange(16) + 1)
    return c


def hybrid_step(nc, x_prompt, x_sample, cache_k, cache_v, cache_kidx, state_pool, page_table, c_prompt, c_sample,
                norm_mix_g, norm_ffn_g, w_mod, b_mod, dsa_w_in, dsa_w_o, pool_w, pool_scale, w_up, w_down,
                final_norm_g, consts, y_prompt, y_sample, k_p, v_p, ki_p, pool_p, k_s, v_s, ki_s, pool_s):
    ctx = ExitStack()
    with ctx:
        top = [(nc.sbuf_base + 63) // 64 * 64]

        def at(name, shape, dt, offset):
            assert offset + 4 * int(np.prod(shape[1:])) <= nc.sbuf_usable_end, name
            return nc.alloc_sbuf_tensor_at(name, shape, dt, offset=offset)

        def sb(name, shape, dt=F32):
            offset = top[0]
            top[0] = (offset + 4 * int(np.prod(shape[1:])) + 31) // 32 * 32
            return at(name, shape, dt, offset)

        def region(start):
            here = [start]

            def put(name, shape, dt=F32):
                offset = here[0]
                here[0] = (offset + 4 * int(np.prod(shape[1:])) + 31) // 32 * 32
                return at(name, shape, dt, offset)
            return put

        cst = sb("cst", [P, C_ALL])
        mod = sb("mod", [P, 2, NVEC, 9])
        gains = sb("gains", [P, 48])
        small = sb("small", [P, 64])
        wiq = sb("wiq", [P, TILES, IH])
        x = sb("x", [P, KT8, ROWS])
        wraw = sb("wraw", [P, 2, UNIT])
        whi = sb("whi", [P, 2, UNIT], F32R)
        wlo = sb("wlo", [P, 2, UNIT], F32R)
        r1 = top[0]
        hhi = sb("hhi", [P, KT8, ROWS], F32R)
        hlo = sb("hlo", [P, KT8, ROWS], F32R)
        s1 = top[0]
        qt = sb("qt", [P, HEADS, ROWS])
        kt = sb("kt", [P, KV, ROWS])
        vr = sb("vr", [P, TILES + 1, KW])
        qi = sb("qi", [P, IH // 2, ROWS])
        kiwi = top[0]
        ki2 = sb("ki2", [P, ROWS])
        wi = sb("wi", [IH, ROWS])
        vt = at("vt", [P, KV, ROWS], F32, kiwi)
        put = region(s1)
        mraw = put("mraw", [P, 4, KT8, 256])
        xrow = put("xrow", [P, 4, D])
        vrow = put("vrow", [P, 2, P])
        crow = put("crow", [9, D])
        cexp = put("cexp", [P, KT8 * 9])
        csum = put("csum", [P, KT8 * 9])
        crec = put("crec", [P, KT8 * 9])
        csil = put("csil", [P, KT8, 9])
        bmod = put("bmod", [P, 96])
        mrow = put("mrow", [9, 2, 256])
        put = region(s1)
        hf = put("hf", [P, KT8, ROWS])
        sq = put("sq", [P, 4, CW])
        nv = put("nv", [P, NC, CW])
        nr = put("nr", [P, NC, CW])
        ny = put("ny", [P, NC, CW])
        rst = put("rst", [P, ROWS])
        tt = put("tt", [P, 4, CW])
        ts = put("ts", [P, KT8, NS])
        put = region(s1)
        hidh = put("hidh", [P, 4, ROWS], F32R)
        hidl = put("hidl", [P, 4, ROWS], F32R)
        relu = put("relu", [P, NC, CW])
        squ = put("squ", [P, NC, CW])
        put = region(s1 + 4 * KT8 * ROWS)
        ext = put("ext", [P, 4, 16 + SEQ])
        exs = put("exs", [P, KT8, NB, PS + DT])
        exa = put("exa", [P, 4, 2, NB, PS + DT])
        pooled = put("pooled", [P, 2, ROWS])
        headcol = put("headcol", [P, 16])
        exs_out = put("exs_out", [P, KT8, NB * PS])
        prow = put("prow", [NB * PS, D])
        srow = at("srow", [NB * PS, D], F32, prow.manual_sbuf_range[0])
        prow_p = at("prow_p", [PS, D], F32, prow.manual_sbuf_range[0])
        put = region(r1)
        yrow = put("yrow", [P, 2, D])
        put = region(r1)
        krow = put("krow", [P, 2, 328])
        kir = put("kir", [P, NB, PAGES, ID])
        vn = at("vn", [DT, NB, KW], F32, kir.manual_sbuf_range[0])
        kpg = put("kpg", [P, 2, PAGES, KW])
        vpg = put("vpg", [P, 2, PAGES, KW])
        kit = put("kit", [ID, 2, PAST])
        kts = put("kts", [P, 2, KV, PAST])
        ssm = put("ssm", [P, 2, SL])
        scs = put("scs", [NS, SL + 7])
        msk = put("msk", [NS, SL])
        mks = put("mks", [P, 2, SL])
        wsel = put("wsel", [P, 2, NS])
        pts = put("pts", [P, 2, PAGES + 1, P])
        qis = put("qis", [ID, NB, IH * DT])
        qit = put("qit", [ID, IH // 2, NS])
        qps = put("qps", [P, NB, KV, HEADS * DT])
        ptb = put("ptb", [1, NB * PAGES], I32)
        assert ptb.manual_sbuf_range[1] <= s1, ptb.manual_sbuf_range
        put = region(r1)
        score = put("score", [P, SEQ])
        mask = put("mask", [P, SEQ])
        rl = put("rl", [P, 3, 512])
        ss = put("ss", [P, 2, SEQ])
        pt = put("pt", [P, TILES, GROUP * P])
        assert pt.manual_sbuf_range[1] <= s1

        pair = [ctx.enter_context(nc.psum_tensor(f"pair{i}", [P, 2, 512], F32)) for i in range(4)]

        def bank(i):
            return pair[i // 2][:, i % 2, :]

        def wide(i):
            return pair[i][:, :, :].rearrange("p a b -> p (a b)")

        ident = cst[:, C_ID:C_ID + P]

        def ident_of(n):
            return cst[0:n, C_ID:C_ID + n]

        def sem(name):
            return ctx.enter_context(nc.semaphore(name))

        cst_in, vrow_in, crow_in = sem("cst_in"), sem("vrow_in"), sem("crow_in")
        xrow_in = [sem(f"xrow_in{i}") for i in range(4)]
        mraw_in = [sem(f"mraw_in{i}") for i in range(4)]
        raw_in = [sem(f"raw_in{i}") for i in range(2)]
        gains_t, gains_done, crow_t, cexp_done, csil_done = (sem(n) for n in (
            "gains_t", "gains_done", "crow_t", "cexp_done", "csil_done"))
        xt_ready, xt_done = sem("xt_ready"), sem("xt_done")
        mod_mm, mod_row, mod_t, mod_done = sem("mod_mm"), sem("mod_row"), sem("mod_t"), sem("mod_done")
        hi_ready, lo_ready = sem("hi_ready"), sem("lo_ready")
        up_ready, up_empty = sem("up_ready"), sem("up_empty")
        down_ready, down_empty = sem("down_ready"), sem("down_empty")
        square_done, hid_square, hid_ready = sem("square_done"), sem("hid_square"), sem("hid_ready")
        sq_ready, sq_used, stat_empty, nr_ready, ny_ready = (sem(n) for n in (
            "sq_ready", "sq_used", "stat_empty", "nr_ready", "ny_ready"))
        t_ready, hh_ready = sem("t_ready"), sem("hh_ready")
        vchain, achain, pchain = sem("vchain"), sem("achain"), sem("pchain")
        vt_t, vr_done = sem("vt_t"), sem("vr_done")
        out_st = sem("out_st")
        krow_t, krow_done, krow_wi = sem("krow_t"), sem("krow_done"), sem("krow_wi")
        krow_st = [sem(f"krow_st{i}") for i in range(2)]
        pt_in, ki_in, qit_in, vn_in, vs_st = sem("pt_in"), sem("ki_in"), sem("qit_in"), sem("vn_in"), sem("vs_st")
        kpg_in = [sem(f"kpg_in{i}") for i in range(2)]
        vpg_in = [sem(f"vpg_in{i}") for i in range(2)]
        kit_t, kit_done, logit_done, srelu_done = sem("kit_t"), sem("kit_done"), sem("logit_done"), sem("srelu_done")
        wb_done, wsel_done, sscore_done, qprep = sem("wb_done"), sem("wsel_done"), sem("sscore_done"), sem("qprep")
        round_step = sem("round_step")
        topk_step, smask_done, mk_mm, mk_done = sem("topk_step"), sem("smask_done"), sem("mk_mm"), sem("mk_done")
        kts_t, kts_done, sqk_done = sem("kts_t"), sem("kts_done"), sem("sqk_done")
        sneg_done, sexp_done, sp_done = sem("sneg_done"), sem("sexp_done"), sem("sp_done")
        spt_t, spt_done, spv_done = sem("spt_t"), sem("spt_done"), sem("spv_done")
        lg_ready, lg_relu, lg_used = sem("lg_ready"), sem("lg_relu"), sem("lg_used")
        mask_done = sem("mask_done")
        qk_ready, neg_done, exp_done, rec_done, prob_done = (sem(n) for n in (
            "qk_ready", "neg_done", "exp_done", "rec_done", "prob_done"))
        p_t, p_copied, pv_ready, pv_empty = sem("p_t"), sem("p_copied"), sem("pv_ready"), sem("pv_empty")
        split_hi, vlo, gated, lo_done = sem("split_hi"), sem("vlo"), sem("gated"), sem("lo_done")
        ext_pad, exs_new = sem("ext_pad"), sem("exs_new")
        ext_ready, pooled_done, pooled_hi = sem("ext_ready"), sem("pooled_done"), sem("pooled_hi")
        srow_in, srow_t, srow_done = sem("srow_in"), sem("srow_t"), sem("srow_done")
        pstate_t, pstate_done = sem("pstate_t"), sem("pstate_done")
        y_t, y_copied = sem("y_t"), sem("y_copied")
        yst = [sem(f"yst{i}") for i in range(2)]

        counts = {"v": 0, "a": 0, "p": 0}

        def chain(eng, ins, key, signal):
            counts[key] += 1
            ins.then_inc(signal, 1)
            eng.wait_ge(signal, counts[key])

        def rounds(dve, values, m8, n):
            with dve.Fori(0, n // 4):
                dve.sem_clear(round_step)
                for r in range(4):
                    if r:
                        dve.wait_ge(round_step, 2 * r)
                    dve.max(m8, values).then_inc(round_step, 1)
                    dve.wait_ge(round_step, 2 * r + 1)
                    dve.match_replace(values, m8, values, TAKEN).then_inc(round_step, 1)
                dve.wait_ge(round_step, 8)

        def raw_count(u):
            return 16 * (u // 2 + 1) + (16 if u % 2 == 0 and u >= 16 else 0)

        def load_unit(sp, u, src, slot, first=False):
            if not first:
                sp.wait_ge(hi_ready, u - 1)
                sp.wait_ge(lo_ready, u - 1)
            for dst, s in src:
                sp.dma_start(dst, s).then_inc(raw_in[slot], 16)

        def raw8(slot):
            return wraw[:, slot, :].rearrange("p (k c) -> p k c", k=KT8)

        def split_unit_hi(act, u, slot, landed, free):
            act.wait_ge(raw_in[slot], landed)
            if free is not None:
                act.wait_ge(*free)
            act.activation(whi[:, slot, :], wraw[:, slot, :], ACT.Copy).then_inc(hi_ready, 1)

        def split_unit_lo(pool, u, slot):
            pool.wait_ge(hi_ready, u + 1)
            pool.tensor_tensor(wlo[:, slot, :], wraw[:, slot, :], whi[:, slot, :], ALU.subtract).then_inc(lo_ready, 1)

        def products(pe, out, slot, w, cols, ks, hi, lo, c):
            wh = whi[:, slot, :].rearrange("p (k c) -> p k c", c=w)
            wl = wlo[:, slot, :].rearrange("p (k c) -> p k c", c=w)
            r = slice(c * CW, (c + 1) * CW)
            for n, (kw, kr) in enumerate(ks):
                a, b = wh[:, kw, cols], wl[:, kw, cols]
                pe.matmul(out, a, hi[:, kr, r], start=(n == 0), stop=False)
                pe.matmul(out, a, lo[:, kr, r], start=False, stop=False)
                last = pe.matmul(out, b, hi[:, kr, r], start=False, stop=(n == len(ks) - 1))
            return last

        def residual(dve, g, c, d, layer, gate):
            dve.wait_ge(down_ready, g + 1)
            dve.wait_ge(down_empty, g)
            ps = bank(3 + c)
            n = CW if c < 2 else LASTP
            xs = x[:, d, c * CW:c * CW + n]
            ins = dve.scalar_tensor_tensor(out=xs, in0=ps[:, 0:n], scalar=mod[:, layer, gate + d, 0:1], in1=xs,
                                           op0=ALU.mult, op1=ALU.add)
            if c == 2:
                tmp = small[:, 32:64]
                dve.tensor_tensor(tmp.rearrange("p (b t) -> p b t", t=DT),
                                  ps[:, LASTP:CW].rearrange("p (b t) -> p b t", t=DT),
                                  mod[:, layer, gate + d, 1:9].unsqueeze(2).to_broadcast([P, NB, DT]),
                                  ALU.mult).then_inc(gated, 1)
                return True
            ins.then_inc(down_empty, 1)
            return False

        def residual_end(dve, gate_count, d):
            dve.wait_ge(gated, gate_count)
            xs = x[:, d, SEQ:ROWS]
            dve.tensor_tensor(xs, xs, small[:, 32:64], ALU.add).then_inc(down_empty, 1)

        mod_halves = NVEC // 2
        NH = 2 * mod_halves
        with nc.Block() as block:
            @block.sync
            def _(sp):
                sp.dma_start(cst[:], consts).then_inc(cst_in, 16)
                sp.dma_start(crow[0:1, :], c_prompt).then_inc(crow_in, 16)
                sp.dma_start(crow[1:9, :], c_sample).then_inc(crow_in, 16)

                def load_mod(n):
                    if n >= 4:
                        sp.wait_ge(mod_mm, n - 3)
                    layer, m = divmod(n, mod_halves)
                    sp.dma_start(mraw[:, n % 4], w_mod[layer, :, m * 256:(m + 1) * 256].rearrange(
                        "(k p) c -> p k c", p=P)).then_inc(mraw_in[n % 4], 16)

                for n in range(4):
                    load_mod(n)
                for i, src in enumerate((norm_mix_g, norm_ffn_g)):
                    sp.dma_start(vrow[16 * i:16 * i + 16, 0, :],
                                 src.rearrange("l (a b) -> (l a) b", b=P)).then_inc(vrow_in, 16)
                sp.dma_start(vrow[32:40, 0, :], final_norm_g.rearrange("(a b) -> a b", b=P)).then_inc(vrow_in, 16)
                sp.dma_start(vrow[40:48, 0, :], pool_scale.rearrange("l (a b) -> (l a) b", b=P)).then_inc(vrow_in, 16)
                sp.dma_start(vrow[0:96, 1, :], b_mod.rearrange("l (a b) -> (l a) b", b=P)).then_inc(vrow_in, 16)
                for i in range(TILES + 1):
                    if i >= 4:
                        sp.wait_ge(xt_ready, i - 3)
                    src = x_prompt[0, i * P:(i + 1) * P, :] if i < TILES else x_sample.rearrange("b t d -> (b t) d")
                    sp.dma_start(xrow[0:src.shape[0], i % 4, :], src).then_inc(xrow_in[i % 4], 16)
                    if 4 + i < NH:
                        load_mod(4 + i)
                for n in range(4 + TILES + 1, NH):
                    load_mod(n)
                for u in range(2):
                    load_unit(sp, u, [(raw8(u % 2), dsa_w_in[0, :, u_in_cols(u)].rearrange(
                        "(k p) c -> p k c", p=P))], u % 2, first=True)

            @block.tensor
            def _(pe):
                pe.wait_ge(cst_in, 16)
                pe.wait_ge(crow_in, 32)
                for k in range(KT8):
                    ins = pe.transpose(bank(6)[:, 9 * k:9 * k + 9], crow[0:9, k * P:(k + 1) * P], ident_of(9))
                ins.then_inc(crow_t, 1)
                pe.wait_ge(vrow_in, 80)
                pe.transpose(bank(7)[:, 0:48], vrow[0:48, 0, :], ident_of(48)).then_inc(gains_t, 1)
                pe.transpose(bank(7)[:, 128:224], vrow[0:96, 1, :], ident_of(96)).then_inc(gains_t, 1)
                pe.wait_ge(csil_done, 1)
                pe.wait_ge(gains_done, 2)

                def tile_of_x(i):
                    pe.wait_ge(xrow_in[i % 4], 16 * (i // 4 + 1))
                    if i >= 2:
                        pe.wait_ge(xt_done, i - 1)
                    n = P if i < TILES else NS
                    for k in range(KT8):
                        ins = pe.transpose(wide(i % 2)[:, k * P:k * P + n], xrow[0:n, i % 4, k * P:(k + 1) * P],
                                           ident_of(n))
                    ins.then_inc(xt_ready, 1)

                def mod_turn(n):
                    pe.wait_ge(mod_row, n + 1)
                    if n >= 2:
                        pe.wait_ge(mod_done, n - 1)
                    for a in range(2):
                        ins = pe.transpose(bank(6 + n % 2)[:, 9 * a:9 * a + 9], mrow[0:9, n % 2, a * P:(a + 1) * P],
                                           ident_of(9))
                    ins.then_inc(mod_t, 1)

                for n in range(NH):
                    pe.wait_ge(mraw_in[n % 4], 16 * (n // 4 + 1))
                    if n >= 2:
                        pe.wait_ge(mod_row, n - 1)
                    for k in range(KT8):
                        ins = pe.matmul(bank(4 + n % 2)[0:9, 0:256], csil[:, k, :], mraw[:, n % 4, k, :],
                                        start=(k == 0), stop=(k == KT8 - 1))
                    ins.then_inc(mod_mm, 1)
                    if n >= 1:
                        mod_turn(n - 1)
                    if n < TILES + 1:
                        tile_of_x(n)
                mod_turn(NH - 1)

            @block.scalar
            def _(act):
                act.wait_ge(crow_t, 1)
                act.activation(cexp[:], bank(6)[:, 0:72], ACT.Exp, scale=-1.0).then_inc(cexp_done, 1)
                for i in range(TILES + 1):
                    act.wait_ge(xt_ready, i + 1)
                    n = P if i < TILES else NS
                    act.activation(x[:, :, i * P:i * P + n],
                                   wide(i % 2).rearrange("p (k c) -> p k c", k=KT8)[:, :, 0:n],
                                   ACT.Copy).then_inc(xt_done, 1)

            @block.vector
            def _(dve):
                dve.wait_ge(cexp_done, 1)
                chain(dve, dve.tensor_scalar(csum[:], cexp[:], 1.0, None, ALU.add), "v", vchain)
                chain(dve, dve.reciprocal(crec[:], csum[:]), "v", vchain)
                dve.tensor_tensor(csil[:].rearrange("p k b -> p (k b)"), bank(6)[:, 0:72], crec[:],
                                  ALU.mult).then_inc(csil_done, 1)
                dve.wait_ge(gains_t, 2)
                dve.tensor_copy(gains[:], bank(7)[:, 0:48]).then_inc(gains_done, 1)
                dve.tensor_copy(bmod[:], bank(7)[:, 128:224]).then_inc(gains_done, 1)
                dve.wait_ge(gains_done, 2)

                def add_bias(n):
                    layer, m = divmod(n, mod_halves)
                    dve.wait_ge(mod_t, n + 1)
                    dve.tensor_tensor(mod[:, layer, 2 * m:2 * m + 2, :],
                                      bank(6 + n % 2)[:, 0:18].rearrange("p (a b) -> p a b", a=2),
                                      bmod[:, NVEC * layer + 2 * m:NVEC * layer + 2 * m + 2].unsqueeze(2)
                                      .to_broadcast([P, 2, 9]), ALU.add).then_inc(mod_done, 1)

                for n in range(NH):
                    dve.wait_ge(mod_mm, n + 1)
                    if n >= 2:
                        dve.wait_ge(mod_t, n - 1)
                    dve.tensor_copy(mrow[0:9, n % 2, :], bank(4 + n % 2)[0:9, 0:256]).then_inc(mod_row, 1)
                    if n >= 1:
                        add_bias(n - 1)
                add_bias(NH - 1)
                dve.wait_ge(mod_done, NH)
                for layer in range(2):
                    for half in range(2):
                        a = mod[:, layer, 24 * half + 8:24 * half + 16, :]
                        g = gains[:, 16 * half + 8 * layer:16 * half + 8 * layer + 8]
                        dve.scalar_tensor_tensor(out=a, in0=a, scalar=1.0,
                                                 in1=g.unsqueeze(2).to_broadcast([P, 8, 9]),
                                                 op0=ALU.add, op1=ALU.mult)
                a = mod[:, 1, 16:24, :]
                chain(dve, dve.tensor_tensor(a, a, gains[:, 40:48].unsqueeze(2).to_broadcast([P, 8, 9]), ALU.mult),
                      "v", vchain)

        def norm_scalar(act, n, layer, shift, kind):
            for c in range(NC):
                for d in range(KT8):
                    i = 24 * n + 8 * c + d
                    if i >= 4:
                        act.wait_ge(sq_used, i - 3)
                    act.activation(sq[:, i % 4, :], x[:, d, c * CW:(c + 1) * CW], ACT.Square).then_inc(sq_ready, 1)
            for c in range(NC):
                act.wait_ge(nr_ready, 3 * n + c + 1)
                act.activation(ny[:, c, :], nr[:, c, :], ACT.Sqrt).then_inc(ny_ready, 1)
            if kind != "split":
                return
            base = 25 * split_norms[n]
            act.wait_ge(t_ready, base + 1)
            act.activation(hhi[:, :, SEQ:ROWS], ts[:], ACT.Copy).then_inc(hh_ready, 1)
            for d in range(KT8):
                for c in range(NC):
                    i = 3 * d + c
                    w = CW if c < 2 else LASTP
                    act.wait_ge(t_ready, base + i + 2)
                    act.activation(hhi[:, d, c * CW:c * CW + w], tt[:, i % 4, 0:w], ACT.Identity,
                                   bias=mod[:, layer, shift + d, 0:1]).then_inc(hh_ready, 1)

        def norm_tensor(pe, n):
            for c in range(NC):
                if 3 * n + c >= 2:
                    pe.wait_ge(stat_empty, 3 * n + c - 1)
                for d in range(KT8):
                    i = 24 * n + 8 * c + d
                    pe.wait_ge(sq_ready, i + 1)
                    pe.matmul(bank(6 + (3 * n + c) % 2)[:, 0:CW], cst[:, C_ONE:C_ONE + P], sq[:, i % 4, :],
                              start=(d == 0), stop=(d == KT8 - 1)).then_inc(sq_used, 1)

        split_norms = {0: 0, 1: 1, 3: 2}

        def norm_vector(dve, n, layer, shift, kind):
            for c in range(NC):
                dve.wait_ge(sq_used, 24 * n + 8 * (c + 1))
                dve.tensor_scalar(nv[:, c, :], bank(6 + (3 * n + c) % 2)[:, 0:CW], EPS, None,
                                  ALU.add).then_inc(stat_empty, 1)
                dve.wait_ge(stat_empty, 3 * n + c + 1)
                dve.reciprocal(nr[:, c, :], nv[:, c, :]).then_inc(nr_ready, 1)
            for c in range(NC):
                dve.wait_ge(ny_ready, 3 * n + c + 1)
                t = nr[:, c, :]
                chain(dve, dve.tensor_tensor(t, ny[:, c, :], ny[:, c, :], ALU.mult), "v", vchain)
                chain(dve, dve.scalar_tensor_tensor(out=t, in0=t, scalar=-0.5, in1=nv[:, c, :], op0=ALU.mult,
                                                    op1=ALU.mult), "v", vchain)
                chain(dve, dve.scalar_tensor_tensor(out=rst[:, c * CW:(c + 1) * CW], in0=t, scalar=1.5,
                                                    in1=ny[:, c, :], op0=ALU.add, op1=ALU.mult), "v", vchain)
            if kind == "final":
                for d in range(KT8):
                    ins = dve.scalar_tensor_tensor(out=hf[:, d, :], in0=x[:, d, :], scalar=gains[:, 32 + d:33 + d],
                                                   in1=rst[:], op0=ALU.mult, op1=ALU.mult)
                chain(dve, ins, "v", vchain)
                return
            four = lambda a: a.rearrange("p k (b t) -> p k b t", t=DT)
            chain(dve, dve.tensor_tensor(ts[:], x[:, :, SEQ:ROWS], rst[:, SEQ:ROWS].unsqueeze(1)
                                         .to_broadcast([P, KT8, NS]), ALU.mult), "v", vchain)
            for vec, op in ((shift + 8, ALU.mult), (shift, ALU.add)):
                dst = ts[:] if vec != shift or kind == "split" else hf[:, :, SEQ:ROWS]
                for t in range(DT):
                    src = four(ts[:])[:, :, :, t]
                    ins = dve.tensor_tensor(four(dst)[:, :, :, t], src, mod[:, layer, vec:vec + 8, 1:9], op)
                if vec != shift or kind != "split":
                    chain(dve, ins, "v", vchain)
            if kind == "split":
                base = 25 * split_norms[n]
                ins.then_inc(t_ready, 1)
                dve.wait_ge(hh_ready, base + 1)
                dve.tensor_tensor(hlo[:, :, SEQ:ROWS], ts[:], hhi[:, :, SEQ:ROWS], ALU.subtract)

            def scaled(i, out):
                d, c = divmod(i, 3)
                w = CW if c < 2 else LASTP
                return dve.scalar_tensor_tensor(out=out, in0=x[:, d, c * CW:c * CW + w],
                                                scalar=mod[:, layer, shift + 8 + d, 0:1],
                                                in1=rst[:, c * CW:c * CW + w], op0=ALU.mult, op1=ALU.mult)

            def lower(i):
                d, c = divmod(i, 3)
                w = CW if c < 2 else LASTP
                r = slice(c * CW, c * CW + w)
                dve.wait_ge(hh_ready, base + i + 2)
                dve.scalar_tensor_tensor(out=hlo[:, d, r], in0=tt[:, i % 4, 0:w],
                                         scalar=mod[:, layer, shift + d, 0:1], in1=hhi[:, d, r],
                                         op0=ALU.add, op1=ALU.subtract).then_inc(lo_done, 1)

            for i in range(24):
                w = CW if i % 3 < 2 else LASTP
                if kind == "split":
                    if i >= 4:
                        dve.wait_ge(lo_done, 24 * split_norms[n] + i - 3)
                    scaled(i, tt[:, i % 4, 0:w]).then_inc(t_ready, 1)
                    if i >= 2:
                        lower(i - 2)
                else:
                    d, c = divmod(i, 3)
                    r = slice(c * CW, c * CW + w)
                    chain(dve, scaled(i, tt[:, i % 4, 0:w]), "v", vchain)
                    ins = dve.tensor_scalar(hf[:, d, r], tt[:, i % 4, 0:w], mod[:, layer, shift + d, 0:1], None,
                                            ALU.add)
                    if i % 4 == 3 or i == 23:
                        chain(dve, ins, "v", vchain)
            if kind == "split":
                lower(22)
                lower(23)
                dve.wait_ge(lo_done, 24 * split_norms[n] + 24)

        def norm_block(n, layer, shift, kind):
            with nc.Block() as block:
                @block.scalar
                def _(act):
                    norm_scalar(act, n, layer, shift, kind)

                @block.tensor
                def _(pe):
                    norm_tensor(pe, n)

                @block.vector
                def _(dve):
                    norm_vector(dve, n, layer, shift, kind)

        norm_block(0, 0, 0, "split")

        with nc.Block() as block:
            @block.sync
            def _(sp):
                for u in range(2, 16):
                    load_unit(sp, u, [(raw8(u % 2), dsa_w_in[0, :, u_in_cols(u)].rearrange(
                        "(k p) c -> p k c", p=P))], u % 2)
                c0 = QW + 2 * KW + IW
                kiw = dsa_w_in[0, :, c0:c0 + ID].rearrange("(k p) c -> p k c", p=P)
                load_unit(sp, 16, [(raw8(0)[:, :, 0:ID], kiw), (raw8(0)[:, :, ID:2 * ID], kiw)], 0)
                load_unit(sp, 17, [(raw8(1)[:, :, 0:IH],
                                    dsa_w_in[0, :, c0 + ID:c0 + ID + IH].rearrange("(k p) c -> p k c", p=P))], 1)
                for u in range(18, 20):
                    load_unit(sp, u, [(raw8(u % 2), dsa_w_o[0, :, (u - 18) * P:(u - 17) * P].rearrange(
                        "(k p) c -> p k c", p=P))], u % 2)
                sp.wait_ge(vr_done, 6)
                sp.dma_start(v_p[0, 0].rearrange("(i p) g d -> p i (g d)", p=P), vr[:, 0:TILES, :]).then_inc(out_st, 16)
                sp.dma_start(v_s[0].rearrange("b t g d -> (b t) (g d)"), vr[0:NS, TILES, :]).then_inc(vs_st, 16)
                sp.wait_ge(out_st, 16)
                sp.wait_ge(vs_st, 16)

            @block.scalar
            def _(act):
                def part(u):
                    split_unit_hi(act, u, u % 2, raw_count(u), (down_ready, 3 * (u - 1)) if u >= 2 else None)

                def rows_of_v(s):
                    act.wait_ge(vt_t, s + 1)
                    g, i = divmod(s, 2)
                    if s < 4:
                        act.activation(vr[:, 4 * i:4 * i + 4, g * P:(g + 1) * P],
                                       bank(6 + s % 2).rearrange("p (i c) -> p i c", i=4), ACT.Copy).then_inc(vr_done, 1)
                    else:
                        g = s - 4
                        act.activation(vr[0:NS, TILES, g * P:(g + 1) * P], bank(6 + s % 2)[0:NS, 0:P],
                                       ACT.Copy).then_inc(vr_done, 1)

                for u in range(4):
                    part(u)
                for s in range(6):
                    part(4 + s)
                    rows_of_v(s)
                for u in range(10, N_IN):
                    part(u)

            @block.gpsimd
            def _(pool):
                for u in range(N_IN):
                    split_unit_lo(pool, u, u % 2)

            @block.tensor
            def _(pe):
                def rows_of_v(s):
                    pe.wait_ge(down_empty, 6)
                    if s >= 2:
                        pe.wait_ge(vr_done, s - 1)
                    g, i = divmod(s, 2)
                    if s < 4:
                        for a in range(4):
                            t = 4 * i + a
                            ins = pe.transpose(bank(6 + s % 2)[:, a * P:(a + 1) * P], vt[:, g, t * P:(t + 1) * P], ident)
                    else:
                        ins = pe.transpose(bank(6 + s % 2)[0:NS, 0:P], vt[:, s - 4, SEQ:ROWS], ident)
                    ins.then_inc(vt_t, 1)

                for u in range(N_IN):
                    pe.wait_ge(hi_ready, u + 1)
                    pe.wait_ge(lo_ready, u + 1)
                    m = IH if u == 17 else P
                    for c in range(NC):
                        g = G_IN + 3 * u + c
                        if g >= 3:
                            pe.wait_ge(down_empty, g - 2)
                        products(pe, bank(3 + c)[0:m, 0:CW], u % 2, P, slice(0, m),
                                 [(k, k) for k in range(KT8)], hhi, hlo, c).then_inc(down_ready, 1)
                    if 3 <= u < 9:
                        rows_of_v(u - 3)

            @block.vector
            def _(dve):
                for u in range(N_IN):
                    dst, m = u_in_dst(u, vt, kt, qt, qi, ki2, wi)
                    for c in range(NC):
                        g = G_IN + 3 * u + c
                        dve.wait_ge(down_ready, g + 1)
                        if u >= 16:
                            dve.wait_ge(vt_t, 6)
                        dve.tensor_copy(dst[0:m, c * CW:(c + 1) * CW], bank(3 + c)[0:m, 0:CW]).then_inc(down_empty, 1)

        with nc.Block() as block:
            @block.sync
            def _(sp):
                sp.dma_start(ptb[:], page_table.rearrange("b (o n) -> o (b n)", o=1)).then_inc(pt_in, 16)
                sp.dma_start(qit[:], qi[ID:2 * ID, :, SEQ:ROWS]).then_inc(qit_in, 16)
                sp.wait_ge(pt_in, 16)

                pool_pages = cache_k.shape[1]

                def page(b, n):
                    return sp.value_load(ptb[0:1, b * PAGES + n:b * PAGES + n + 1], min_val=0, max_val=pool_pages - 1)

                for b in range(NB):
                    for n in range(PAGES):
                        pg = page(b, n)
                        sp.dma_start(kir[:, b, n, :],
                                     cache_kidx[0, bass.ds(pg, 1), :, :].rearrange("a s d -> (a s) d")).then_inc(ki_in, 16)

                def load_pages(dst, cache, signals, b):
                    for n in range(PAGES):
                        pg = page(b, n)
                        sp.dma_start(dst[:, b % 2, n, :], cache[0, bass.ds(pg, 1)].rearrange("a s g d -> (a s) (g d)")
                                     ).then_inc(signals[b % 2], 16)

                for b in range(2):
                    load_pages(kpg, cache_k, kpg_in, b)
                    load_pages(vpg, cache_v, vpg_in, b)
                for i in range(TILES + 1):
                    sp.wait_ge(krow_done, i + 1)
                    n = P if i < TILES else NS
                    if i < TILES:
                        ko, io = k_p[0, 0, i * P:(i + 1) * P].rearrange("s g d -> s (g d)"), ki_p[0, 0, i * P:(i + 1) * P]
                    else:
                        ko, io = k_s[0].rearrange("b t g d -> (b t) (g d)"), ki_s[0].rearrange("b t d -> (b t) d")
                    sp.dma_start(ko, krow[0:n, i % 2, 0:KW]).then_inc(krow_st[i % 2], 16)
                    sp.dma_start(io, krow[0:n, i % 2, KW:KW + ID]).then_inc(krow_st[i % 2], 16)
                sp.wait_ge(kit_t, NB)
                sp.dma_start(vn[:], v_s[0].rearrange("b t g d -> t b (g d)")).then_inc(vn_in, 16)
                for b in range(2, NB):
                    sp.wait_ge(kts_t, 2 * b - 2)
                    load_pages(kpg, cache_k, kpg_in, b)
                for b in range(2, NB):
                    sp.wait_ge(spv_done, b - 1)
                    load_pages(vpg, cache_v, vpg_in, b)
                sp.wait_ge(krow_st[0], 32 * 5)
                sp.wait_ge(krow_st[1], 32 * 4)

            @block.tensor
            def _(pe):
                for i in range(TILES + 1):
                    n = P if i < TILES else NS
                    if i >= 2:
                        pe.wait_ge(krow_done, i - 1)
                    o = bank(6 + i % 2)
                    for g in range(KV):
                        pe.transpose(o[0:n, g * P:(g + 1) * P], kt[:, g, i * P:i * P + n], ident)
                    pe.transpose(o[0:n, KW:KW + ID], ki2[0:ID, i * P:i * P + n], ident_of(ID))
                    pe.transpose(o[0:n, KW + ID:KW + ID + IH], wi[0:IH, i * P:i * P + n],
                                 ident_of(IH)).then_inc(krow_t, 1)
                pe.wait_ge(krow_done, TILES + 1)
                pe.wait_ge(ki_in, 16 * NB * PAGES)
                pe.wait_ge(qprep, 8)
                for b in range(NB + 1):
                    if b < NB:
                        if b >= 2:
                            pe.wait_ge(kit_done, b - 1)
                        for n in range(PAGES):
                            ins = pe.transpose(bank(6 + b % 2)[0:ID, n * P:(n + 1) * P], kir[:, b, n, :], ident)
                        ins.then_inc(kit_t, 1)
                    if b >= 1:
                        a = b - 1
                        pe.wait_ge(kit_done, a + 1)
                        j = 32 * (a % 4)
                        o = pair[1 + a // 4]
                        pe.matmul(o[j:j + 32, 0, :], qis[:, a, :], kit[:, a % 2, :], start=True, stop=True)
                        pe.matmul(o[j:j + 32, 1, 0:DT], qis[:, a, :], ki2[0:ID, SEQ + DT * a:SEQ + DT * a + DT],
                                  start=True, stop=True).then_inc(logit_done, 1)
                pe.matmul(bank(6)[:, 0:NS], cst[0:IH, C_EH:C_EH + P], wi[0:IH, SEQ:ROWS], start=True,
                          stop=True).then_inc(wb_done, 1)
                pe.wait_ge(wsel_done, 2)
                pe.wait_ge(srelu_done, 2)
                for a, (lo, hi) in enumerate(((0, PAST), (PAST, SL))):
                    for g in range(2):
                        ins = pe.matmul(pair[0][0:NS, a, 0:hi - lo], wsel[:, g, :], ssm[:, g, lo:hi], start=(g == 0),
                                        stop=(g == 1))
                ins.then_inc(sscore_done, 1)
                pe.wait_ge(qprep, 11)
                for b in range(NB + 1):
                    if b < NB:
                        pe.wait_ge(kpg_in[b % 2], 16 * PAGES * (b // 2 + 1))
                        for g in range(KV):
                            if b >= 1:
                                pe.wait_ge(kts_done, 2 * b - 1 + g)
                            for n in range(PAGES):
                                ins = pe.transpose(bank(6 + g)[:, n * P:(n + 1) * P],
                                                   kpg[:, b % 2, n, g * P:(g + 1) * P], ident)
                            ins.then_inc(kts_t, 1)
                    if b >= 1:
                        a = b - 1
                        pe.wait_ge(kts_done, 2 * a + 2)
                        j = 32 * (a % 4)
                        o = pair[1 + a // 4]
                        for g in range(KV):
                            pe.matmul(o[j:j + 32, 0, :], qps[:, a, g, :], kts[:, a % 2, g, :], start=(g == 0),
                                      stop=(g == KV - 1))
                        for g in range(KV):
                            ins = pe.matmul(o[j:j + 32, 1, 0:DT], qps[:, a, g, :],
                                            kt[:, g, SEQ + DT * a:SEQ + DT * a + DT], start=(g == 0),
                                            stop=(g == KV - 1))
                        ins.then_inc(sqk_done, 1)
                pe.wait_ge(smask_done, 1)
                for g in range(2):
                    if g == 1:
                        pe.wait_ge(mk_done, 1)
                    rb = cst[0:NS, C_RB + P * g:C_RB + P * (g + 1)]
                    pe.matmul(pair[0][:, 0, :], rb, msk[:, 0:PAST], start=True, stop=True)
                    pe.matmul(pair[0][:, 1, 0:DT], rb, msk[:, PAST:SL], start=True, stop=True).then_inc(mk_mm, 1)
                for g in range(2):
                    pe.wait_ge(sp_done, g + 1)
                    if g == 1:
                        pe.wait_ge(spt_done, 2)
                    for n in range(PAGES):
                        ins = pe.transpose(bank(6)[:, n * P:(n + 1) * P], ssm[:, g, n * P:(n + 1) * P], ident)
                    ins.then_inc(spt_t, 1)
                    pe.transpose(bank(7)[0:DT, 0:P], ssm[:, g, PAST:SL], ident).then_inc(spt_t, 1)
                pe.wait_ge(mk_done, 2)
                pe.wait_ge(vn_in, 16)
                for b in range(NB):
                    G, j = divmod(b, 4)
                    pe.wait_ge(vpg_in[b % 2], 16 * PAGES * (b // 2 + 1))
                    pe.wait_ge(spt_done, 2 * G + 2)
                    for g in range(KV):
                        o = bank(0)[:, (2 * b + g) * 16:(2 * b + g + 1) * 16]
                        c0 = 32 * j + 16 * g
                        for n in range(PAGES):
                            pe.matmul(o, vpg[:, b % 2, n, g * P:(g + 1) * P], pts[:, G, n, c0:c0 + 16],
                                      start=(n == 0), stop=False)
                        ins = pe.matmul(o, vn[:, b, g * P:(g + 1) * P], pts[0:DT, G, PAGES, c0:c0 + 16],
                                        start=False, stop=True)
                    ins.then_inc(spv_done, 1)

            @block.scalar
            def _(act):
                for i in range(TILES + 1):
                    n = P if i < TILES else NS
                    act.wait_ge(krow_t, i + 1)
                    if i >= 2:
                        act.wait_ge(krow_st[i % 2], 32 * (i // 2))
                        act.wait_ge(krow_wi, min(i - 1, TILES))
                    act.activation(krow[0:n, i % 2, :], bank(6 + i % 2)[0:n, 0:328], ACT.Copy).then_inc(krow_done, 1)
                for b in range(NB):
                    act.wait_ge(kit_t, b + 1)
                    if b >= 2:
                        act.wait_ge(logit_done, b - 1)
                    act.activation(kit[:, b % 2, :], bank(6 + b % 2)[0:ID, :], ACT.Copy).then_inc(kit_done, 1)
                for g in range(2):
                    act.wait_ge(logit_done, 4 * g + 4)
                    act.activation(ssm[:, g, :], wide(1 + g)[:, 0:SL], ACT.Relu, scale=SC_IDX).then_inc(srelu_done, 1)
                for b in range(NB):
                    for g in range(KV):
                        act.wait_ge(kts_t, 2 * b + g + 1)
                        if b >= 2:
                            act.wait_ge(sqk_done, b - 1)
                        act.activation(kts[:, b % 2, g, :], bank(6 + g), ACT.Copy).then_inc(kts_done, 1)
                for g in range(2):
                    act.wait_ge(sneg_done, g + 1)
                    act.activation(ssm[:, g, :], ssm[:, g, :], ACT.Exp, bias=small[:, 2 + g:3 + g], scale=SC_ATT,
                                   accum_out=small[:, 4 + g:5 + g]).then_inc(sexp_done, 1)
                for g in range(2):
                    act.wait_ge(spt_t, 2 * g + 1)
                    act.activation(pts[:, g, 0:PAGES, :], bank(6).rearrange("p (n c) -> p n c", n=PAGES),
                                   ACT.Copy).then_inc(spt_done, 1)
                    act.wait_ge(spt_t, 2 * g + 2)
                    act.activation(pts[0:DT, g, PAGES, :], bank(7)[0:DT, 0:P], ACT.Copy).then_inc(spt_done, 1)

            @block.vector
            def _(dve):
                for i in range(TILES):
                    dve.wait_ge(krow_done, i + 1)
                    dve.tensor_copy(wiq[:, i, :], krow[:, i % 2, KW + ID:KW + ID + IH]).then_inc(krow_wi, 1)
                for h in range(0, IH, 2):
                    dve.tensor_copy(qis[:, :, h * DT:(h + 1) * DT],
                                    qi[0:ID, h // 2, SEQ:ROWS].rearrange("p (b t) -> p b t", t=DT)).then_inc(qprep, 1)
                dve.wait_ge(qit_in, 16)
                for h in range(1, IH, 2):
                    dve.tensor_copy(qis[:, :, h * DT:(h + 1) * DT],
                                    qit[:, h // 2, :].rearrange("p (b t) -> p b t", t=DT)).then_inc(qprep, 1)
                dve.memset(qps[:], 0.0).then_inc(qprep, 1)
                dve.wait_ge(qprep, 9)
                for g in range(KV):
                    for r in range(GROUP):
                        h = GROUP * g + r
                        ins = dve.tensor_copy(qps[:, :, g, h * DT:(h + 1) * DT],
                                              qt[:, h, SEQ:ROWS].rearrange("p (b t) -> p b t", t=DT))
                    ins.then_inc(qprep, 1)
                dve.wait_ge(wb_done, 1)
                for g in range(2):
                    dve.tensor_tensor(wsel[:, g, :], bank(6)[:, 0:NS], cst[:, C_SEL + 32 * g:C_SEL + 32 * g + 32],
                                      ALU.mult).then_inc(wsel_done, 1)
                dve.wait_ge(sscore_done, 1)
                dve.tensor_copy(scs[:, 0:PAST], pair[0][0:NS, 0, :])
                dve.memset(scs[:, SL:SL + 7], DECOY)
                dve.tensor_tensor(scs[:, PAST:SL], pair[0][0:NS, 1, 0:DT], cst[0:NS, C_CMS:C_CMS + DT],
                                  ALU.add).then_inc(topk_step, 1)
                m8 = small[0:NS, 8:16]
                full, rest = divmod(SAMPLE_K, 8)
                assert rest == 1 and full % 4 == 0
                dve.wait_ge(topk_step, 1)
                rounds(dve, scs[:], m8, full)
                n0 = 1
                dve.wait_ge(topk_step, n0)
                dve.max(m8, scs[:]).then_inc(topk_step, 1)
                dve.wait_ge(topk_step, n0 + 1)
                dve.memset(small[0:NS, 9:16], DECOY).then_inc(topk_step, 1)
                dve.wait_ge(topk_step, n0 + 2)
                dve.match_replace(scs[:], m8, scs[:], TAKEN).then_inc(topk_step, 1)
                dve.wait_ge(topk_step, n0 + 3)
                dve.tensor_scalar(msk[:], scs[:, 0:SL], CUT, NEG, ALU.is_ge, ALU.mult).then_inc(smask_done, 1)
                for g in range(2):
                    dve.wait_ge(mk_mm, g + 1)
                    dve.tensor_copy(mks[:, g, :], wide(0)[:, 0:SL]).then_inc(mk_done, 1)
                dve.wait_ge(mk_done, 2)
                for g in range(2):
                    dve.wait_ge(sqk_done, 4 * g + 4)
                    chain(dve, dve.tensor_tensor_reduce(ssm[:, g, :], wide(1 + g)[:, 0:SL], mks[:, g, :], 1.0, TAKEN,
                                                        ALU.add, ALU.max, small[:, g:g + 1]), "v", vchain)
                    dve.tensor_scalar(small[:, 2 + g:3 + g], small[:, g:g + 1], -SC_ATT, None,
                                      ALU.mult).then_inc(sneg_done, 1)
                for g in range(2):
                    dve.wait_ge(sexp_done, g + 1)
                    chain(dve, dve.reciprocal(small[:, 6 + g:7 + g], small[:, 4 + g:5 + g]), "v", vchain)
                    dve.tensor_scalar(ssm[:, g, :], ssm[:, g, :], small[:, 6 + g:7 + g], None,
                                      ALU.mult).then_inc(sp_done, 1)
                dve.wait_ge(spv_done, NB)
                for g in range(KV):
                    src = bank(0)[:, 0:256].rearrange("p (b g r t) -> p g r b t", g=KV, r=GROUP, t=DT)[:, g]
                    for r in range(GROUP):
                        dve.tensor_copy(qt[:, GROUP * g + r, SEQ:ROWS].rearrange("p (b t) -> p b t", t=DT), src[:, r])

        topk0 = 4
        first_topk = TOPK // P
        idx_tiles = list(range(first_topk, TILES))
        logit_list = [(t, h, s) for t in idx_tiles for h in range(IH) for s in range((P * (t + 1) + 511) // 512)]
        qk_list = [(t, h) for t in range(TILES) for h in range(HEADS)]
        turn_list = [(t, h, a) for t, h in qk_list for a in range((t + 4) // 4)]
        with nc.Block() as block:
            def logits_of(t):
                return [(n, h, s) for n, (tt_, h, s) in enumerate(logit_list) if tt_ == t]

            def turns_of(t, h):
                return [(n, a) for n, (t_, h_, a) in enumerate(turn_list) if (t_, h_) == (t, h)]

            @block.tensor
            def _(pe):
                def logits(t):
                    for n, h, s in logits_of(t):
                        w = min(512, P * (t + 1) - 512 * s)
                        if n >= 2:
                            pe.wait_ge(lg_relu, n - 1)
                        a = ID * (h % 2)
                        pe.matmul(bank(n % 2)[:, 0:w], qi[a:a + ID, h // 2, t * P:(t + 1) * P],
                                  ki2[a:a + ID, 512 * s:512 * s + w], start=True, stop=True).then_inc(lg_ready, 1)

                def qk(n):
                    t, h = qk_list[n]
                    if n >= 2:
                        pe.wait_ge(neg_done, n - 1)
                    L = P * (t + 1)
                    for s in range((L + 511) // 512):
                        w = min(512, L - 512 * s)
                        ins = pe.matmul(pair[1 + n % 2][:, s, 0:w], qt[:, h, t * P:(t + 1) * P],
                                        kt[:, h // GROUP, 512 * s:512 * s + w], start=True, stop=True)
                    ins.then_inc(qk_ready, 1)

                def turn(n):
                    t, h = qk_list[n]
                    pe.wait_ge(prob_done, n + 1)
                    for m, a in turns_of(t, h):
                        if m >= 1:
                            pe.wait_ge(p_copied, m)
                        for j in range(4 * a, min(4 * a + 4, t + 1)):
                            ins = pe.transpose(bank(6)[:, (j - 4 * a) * P:(j - 4 * a + 1) * P],
                                               ss[:, n % 2, j * P:(j + 1) * P], ident)
                        ins.then_inc(p_t, 1)

                def pv(n):
                    t, h = qk_list[n]
                    g = h // GROUP
                    m = 2 * t + g
                    pe.wait_ge(p_copied, turns_of(t, h)[-1][0] + 1)
                    if m >= 1:
                        pe.wait_ge(pv_empty, m)
                    for j in range(t + 1):
                        ins = pe.matmul(bank(7), vr[:, j, g * P:(g + 1) * P], pt[:, j, :], start=(j == 0), stop=(j == t))
                    ins.then_inc(pv_ready, 1)

                for n, (t, h) in enumerate(qk_list):
                    qk(n)
                    if n >= 1:
                        turn(n - 1)
                        if n % GROUP == 0:
                            pv(n - 1)
                    if h == HEADS - 1 and t + 1 in idx_tiles:
                        logits(t + 1)
                turn(len(qk_list) - 1)
                pv(len(qk_list) - 1)

            @block.scalar
            def _(act):
                def relus(t):
                    for n, h, s in logits_of(t):
                        w = min(512, P * (t + 1) - 512 * s)
                        act.wait_ge(lg_ready, n + 1)
                        if n >= 3:
                            act.wait_ge(lg_used, n - 2)
                        act.activation(rl[:, n % 3, 0:w], bank(n % 2)[:, 0:w], ACT.Relu,
                                       scale=SC_IDX).then_inc(lg_relu, 1)

                def copies(n):
                    t, h = qk_list[n]
                    for m, a in turns_of(t, h):
                        act.wait_ge(p_t, m + 1)
                        k = min(4, t + 1 - 4 * a)
                        if h % GROUP == 0 and 2 * t + h // GROUP >= 1:
                            act.wait_ge(pv_ready, 2 * t + h // GROUP)
                        act.activation(pt[:, 4 * a:4 * a + k, (h % GROUP) * P:(h % GROUP + 1) * P],
                                       bank(6)[:, 0:k * P].rearrange("p (j c) -> p j c", j=k),
                                       ACT.Copy).then_inc(p_copied, 1)

                for n, (t, h) in enumerate(qk_list):
                    L = P * (t + 1)
                    act.wait_ge(neg_done, n + 1)
                    act.activation(ss[:, n % 2, 0:L], ss[:, n % 2, 0:L], ACT.Exp, bias=small[:, 4 + n % 2:5 + n % 2],
                                   scale=SC_ATT, accum_out=small[:, 2 + n % 2:3 + n % 2]).then_inc(exp_done, 1)
                    if n >= 1:
                        copies(n - 1)
                    if h == HEADS - 1 and t + 1 in idx_tiles:
                        relus(t + 1)
                copies(len(qk_list) - 1)

            @block.gpsimd
            def _(pool):
                for n, (t, h) in enumerate(qk_list):
                    L = P * (t + 1)
                    pool.wait_ge(rec_done, n + 1)
                    pool.tensor_scalar(ss[:, n % 2, 0:L], ss[:, n % 2, 0:L], small[:, 6 + n % 2:7 + n % 2], None,
                                       ALU.mult).then_inc(prob_done, 1)

            @block.vector
            def _(dve):
                done = [0]

                def select(t):
                    L = P * (t + 1)
                    for n, h, s in logits_of(t):
                        w = min(512, L - 512 * s)
                        dve.wait_ge(lg_relu, n + 1)
                        if h:
                            dve.wait_ge(lg_used, n - (L + 511) // 512 + 1)
                        sc = score[:, 512 * s:512 * s + w]
                        if h == 0:
                            ins = dve.tensor_scalar(sc, rl[:, n % 3, 0:w], wiq[:, t, 0:1], None, ALU.mult)
                        else:
                            ins = dve.scalar_tensor_tensor(out=sc, in0=rl[:, n % 3, 0:w], scalar=wiq[:, t, h:h + 1],
                                                           in1=sc, op0=ALU.mult, op1=ALU.add)
                        ins.then_inc(lg_used, 1)
                    dve.wait_ge(lg_used, logits_of(t)[-1][0] + 1)
                    n0 = topk0 + done[0] + 1
                    sc = score[:, t * P:L]
                    dve.tensor_tensor(sc, sc, cst[:, C_CM:C_CM + P], ALU.add).then_inc(topk_step, 1)
                    m8 = small[:, 8:16]
                    dve.wait_ge(topk_step, n0)
                    rounds(dve, score[:, 0:L], m8, TOPK // 8)
                    done[0] += 1
                    chain(dve, dve.tensor_scalar(mask[:, 0:L], score[:, 0:L], CUT, NEG, ALU.is_ge, ALU.mult),
                          "v", vchain)

                def recip(n):
                    dve.wait_ge(exp_done, n + 1)
                    dve.reciprocal(small[:, 6 + n % 2:7 + n % 2], small[:, 2 + n % 2:3 + n % 2]).then_inc(rec_done, 1)

                def take_pv(n):
                    t, h = qk_list[n]
                    g = h // GROUP
                    dve.wait_ge(pv_ready, 2 * t + g + 1)
                    dve.tensor_copy(qt[:, GROUP * g:GROUP * (g + 1), t * P:(t + 1) * P],
                                    bank(7).rearrange("p (r c) -> p r c", r=GROUP)).then_inc(pv_empty, 1)

                for n, (t, h) in enumerate(qk_list):
                    L = P * (t + 1)
                    if h == 0:
                        if t < first_topk:
                            if t:
                                dve.memset(mask[:, 0:t * P], 0.0)
                            chain(dve, dve.tensor_copy(mask[:, t * P:L], cst[:, C_CM:C_CM + P]), "v", vchain)
                        else:
                            select(t)
                    dve.wait_ge(qk_ready, n + 1)
                    if n >= 2:
                        dve.wait_ge(p_t, turns_of(*qk_list[n - 2])[-1][0] + 1)
                    chain(dve, dve.tensor_tensor_reduce(ss[:, n % 2, 0:L], wide(1 + n % 2)[:, 0:L], mask[:, 0:L], 1.0,
                                                        TAKEN, ALU.add, ALU.max, small[:, n % 2:n % 2 + 1]),
                          "v", vchain)
                    dve.tensor_scalar(small[:, 4 + n % 2:5 + n % 2], small[:, n % 2:n % 2 + 1], -SC_ATT, None,
                                      ALU.mult).then_inc(neg_done, 1)
                    recip(n)
                    if n % GROUP == 0 and n >= 1:
                        take_pv(n - 1)
                take_pv(len(qk_list) - 1)

        with nc.Block() as block:
            @block.sync
            def _(sp):
                for u in range(U_O + 2, U_MLP0):
                    load_unit(sp, u, [(raw8(u % 2), dsa_w_o[0, :, (u - U_O) * P:(u - U_O + 1) * P].rearrange(
                        "(k p) c -> p k c", p=P))], u % 2)
                for k in range(2):
                    load_unit(sp, U_MLP0 + k, [(raw8(k), w_up[0, :, k * P:(k + 1) * P].rearrange(
                        "(k p) c -> p k c", p=P))], k)

            @block.scalar
            def _(act):
                for u in range(U_O, U_O + 2):
                    split_unit_hi(act, u, u % 2, raw_count(u), (down_ready, 3 * (u - 1)))
                for k in range(KT8):
                    act.activation(hhi[:, k, :], qt[:, k, :], ACT.Copy).then_inc(split_hi, 1)
                for u in range(U_O + 2, U_MLP0):
                    split_unit_hi(act, u, u % 2, raw_count(u), (down_ready, 3 * (u - 1)))

            @block.gpsimd
            def _(pool):
                for u in range(U_O, U_MLP0):
                    split_unit_lo(pool, u, u % 2)

            @block.tensor
            def _(pe):
                pe.wait_ge(vlo, KT8)
                for u in range(U_O, U_MLP0):
                    pe.wait_ge(hi_ready, u + 1)
                    pe.wait_ge(lo_ready, u + 1)
                    for c in range(NC):
                        g = G_O + 3 * (u - U_O) + c
                        pe.wait_ge(down_empty, g - 2)
                        products(pe, bank(3 + c)[:, 0:CW], u % 2, P, slice(0, P),
                                 [(k, k) for k in range(KT8)], hhi, hlo, c).then_inc(down_ready, 1)

            @block.vector
            def _(dve):
                for k in range(KT8):
                    dve.wait_ge(split_hi, k + 1)
                    dve.tensor_tensor(hlo[:, k, :], qt[:, k, :], hhi[:, k, :], ALU.subtract).then_inc(vlo, 1)
                for d in range(KT8):
                    for c in range(NC):
                        if residual(dve, G_O + 3 * d + c, c, d, 0, 16):
                            residual_end(dve, d + 1, d)

        def mlp_block(layer, u0, g0, gates0):
            h0 = 12 * FB * layer

            with nc.Block() as block:
                @block.sync
                def _(sp):
                    def up_src(first, k):
                        return w_up[layer, :, bass.ds(first + k * P, P)].rearrange("(k p) c -> p k c", p=P)

                    def down_src(first, k):
                        return w_down[layer, bass.ds(first, 512), k * 256:(k + 1) * 256].rearrange(
                            "(k p) c -> p k c", p=P)

                    def load(u_wait, slot, dst, src):
                        sp.wait_ge(hi_ready, u_wait)
                        sp.wait_ge(lo_ready, u_wait)
                        sp.dma_start(dst, src).then_inc(raw_in[slot], 16)

                    def raw4(slot):
                        return wraw[:, slot, :].rearrange("p (k c) -> p k c", k=4)

                    def steps(i, ks):
                        for k in ks:
                            u = u0 + k - 1
                            if k < 4:
                                load(i * 8 + u, k % 2, raw8(k % 2), up_src(i * 512, k))
                            else:
                                load(i * 8 + u, k % 2, raw4(k % 2), down_src(i * 512, k - 4))

                    steps(0, range(2, 8))
                    with sp.Fori(1, FB) as i:
                        steps(i, range(8))
                    if layer == 0:
                        for k in range(2):
                            load(U_POOL + k - 1, k, wraw[:, k, :].rearrange("p (g k c) -> p g k c", g=2, k=2),
                                 pool_w[0, 2 * k:2 * k + 2].rearrange("g (k p) c -> p g k c", p=P))

                @block.scalar
                def _(act):
                    def unit(i, k):
                        landed = raw_count(u0 + k)
                        act.wait_ge(raw_in[k % 2], i * 64 + landed)
                        if k < 2:
                            act.wait_ge(down_ready, i * 24 + (g0 - 6 + 6 * k))
                        elif k < 6:
                            act.wait_ge(up_ready, i * 12 + (h0 + 3 * (k - 1)))
                        else:
                            act.wait_ge(down_ready, i * 24 + (g0 + 6 * (k - 5)))
                        act.activation(whi[:, k % 2, :], wraw[:, k % 2, :], ACT.Copy).then_inc(hi_ready, 1)

                    def hidden(i, f):
                        for c in range(NC):
                            g = h0 + 3 * f + c
                            act.wait_ge(up_ready, i * 12 + (g + 1))
                            if g >= 3:
                                act.wait_ge(hid_ready, i * 12 + (g - 2))
                            elif not isinstance(i, int):
                                act.wait_ge(hid_ready, i * 12)
                            act.activation(relu[:, c, :], bank(c)[:, 0:CW], ACT.Relu).then_inc(up_empty, 1)
                            act.wait_ge(up_empty, i * 12 + (g + 1))
                            act.activation(hidh[:, f, c * CW:(c + 1) * CW], relu[:, c, :],
                                           ACT.Square).then_inc(square_done, 1)

                    def steps(i, ahead):
                        for f in range(4):
                            hidden(i, f)
                            unit(i, f + 2)
                        unit(i, 6)
                        unit(i, 7)
                        if ahead:
                            unit(i + 1, 0)
                            unit(i + 1, 1)

                    unit(0, 0)
                    unit(0, 1)
                    steps(0, True)
                    with act.Fori(1, FB - 1) as i:
                        steps(i, True)
                    steps(FB - 1, False)

                @block.gpsimd
                def _(pool):
                    with pool.Fori(0, FB) as i:
                        for k in range(8):
                            pool.wait_ge(hi_ready, i * 8 + (u0 + k + 1))
                            pool.tensor_tensor(wlo[:, k % 2, :], wraw[:, k % 2, :], whi[:, k % 2, :],
                                               ALU.subtract).then_inc(lo_ready, 1)

                @block.tensor
                def _(pe):
                    def weights(i, k):
                        pe.wait_ge(hi_ready, i * 8 + (u0 + k + 1))
                        pe.wait_ge(lo_ready, i * 8 + (u0 + k + 1))

                    def steps(i, first):
                        for f in range(4):
                            weights(i, f)
                            for c in range(NC):
                                g = h0 + 3 * f + c
                                if not (first and g < 3):
                                    pe.wait_ge(up_empty, i * 12 + (g - 2))
                                products(pe, bank(c)[:, 0:CW], f % 2, P, slice(0, P),
                                         [(k, k) for k in range(KT8)], hhi, hlo, c).then_inc(up_ready, 1)
                        for m in range(KT8):
                            if m % 2 == 0:
                                weights(i, 4 + m // 2)
                            for c in range(NC):
                                if m == 0:
                                    pe.wait_ge(hid_ready, i * 12 + (h0 + 10 + c))
                                pe.wait_ge(down_empty, i * 24 + (g0 + 3 * m + c - 2))
                                products(pe, bank(3 + c)[:, 0:CW], (m // 2) % 2, 256,
                                         slice((m % 2) * P, (m % 2 + 1) * P), [(k, k) for k in range(4)],
                                         hidh, hidl, c).then_inc(down_ready, 1)

                    steps(0, True)
                    with pe.Fori(1, FB) as i:
                        steps(i, False)

                @block.vector
                def _(dve):
                    def steps(i):
                        for f in range(4):
                            for c in range(NC):
                                g = h0 + 3 * f + c
                                dve.wait_ge(up_empty, i * 12 + (g + 1))
                                dve.tensor_tensor(squ[:, c, :], relu[:, c, :], relu[:, c, :],
                                                  ALU.mult).then_inc(hid_square, 1)
                                dve.wait_ge(square_done, i * 12 + (g + 1))
                                dve.wait_ge(hid_square, i * 12 + (g + 1))
                                dve.tensor_tensor(hidl[:, f, c * CW:(c + 1) * CW], squ[:, c, :],
                                                  hidh[:, f, c * CW:(c + 1) * CW], ALU.subtract).then_inc(hid_ready, 1)
                        for m in range(KT8):
                            for c in range(NC):
                                if residual_at(i, 24, g0 + 3 * m + c, c, m):
                                    dve.wait_ge(gated, i * 8 + (gates0 + m + 1))
                                    xs = x[:, m, SEQ:ROWS]
                                    dve.tensor_tensor(xs, xs, small[:, 32:64], ALU.add).then_inc(down_empty, 1)

                    def residual_at(i, per, g, c, d):
                        return residual(dve, i * per + g, c, d, layer, 40)

                    with dve.Fori(0, FB) as i:
                        steps(i)

        norm_block(1, 0, 24, "split")
        mlp_block(0, U_MLP0, G_MLP0, KT8)
        norm_block(2, 1, 0, "pool")

        with nc.Block() as block:
            @block.sync
            def _(sp):
                sp.dma_start(srow[:], state_pool[0].rearrange("b s d -> (b s) d")).then_inc(srow_in, 16)
                for k in range(2):
                    load_unit(sp, U_MLP1 + k, [(raw8(k), w_up[1, :, k * P:(k + 1) * P].rearrange(
                        "(k p) c -> p k c", p=P))], k)
                sp.wait_ge(pstate_done, 1)
                sp.dma_start(pool_s[0].rearrange("b s d -> (b s) d"), prow[:]).then_inc(out_st, 16)
                sp.wait_ge(pstate_done, 2)
                sp.dma_start(pool_p[0, 0], prow_p[:]).then_inc(out_st, 16)
                sp.wait_ge(out_st, 48)

            @block.scalar
            def _(act):
                for u in range(U_POOL, U_MLP1):
                    split_unit_hi(act, u, u % 2, raw_count(u), (down_ready, G_POOL))
                act.wait_ge(srow_t, 1)
                for a in range(2):
                    act.activation(exs[:, 4 * a:4 * a + 4, :, 0:PS],
                                   bank(a)[:, 0:480].rearrange("p (k b s) -> p k b s", k=4, b=NB),
                                   ACT.Copy).then_inc(srow_done, 1)

                def upper(d):
                    act.wait_ge(pooled_done, d + 1)
                    act.activation(hhi[:, d, :], pooled[:, d % 2, :], ACT.Copy).then_inc(pooled_hi, 1)

                act.wait_ge(ext_pad, 1)
                for d in range(KT8):
                    if d >= 2:
                        act.wait_ge(pooled_done, d - 1)
                    act.activation(ext[:, d % 2, 16:], hf[:, d, 0:SEQ], ACT.Copy).then_inc(ext_ready, 1)
                    if d >= 1:
                        upper(d - 1)
                    if d == 2:
                        act.wait_ge(pstate_t, 2)
                        act.activation(prow[:], wide(0)[0:120, :], ACT.Copy).then_inc(pstate_done, 1)
                upper(KT8 - 1)
                act.wait_ge(out_st, 32)
                act.activation(prow_p[:], wide(3)[0:PS, :], ACT.Copy).then_inc(pstate_done, 1)

            @block.gpsimd
            def _(pool):
                for u in range(U_POOL, U_MLP1):
                    split_unit_lo(pool, u, u % 2)

            @block.tensor
            def _(pe):
                pe.wait_ge(srow_in, 16)
                for k in range(KT8):
                    ins = pe.transpose(bank(k // 4)[:, (k % 4) * 120:(k % 4 + 1) * 120], srow[:, k * P:(k + 1) * P],
                                       ident_of(120))
                ins.then_inc(srow_t, 1)
                for k in range(KT8):
                    ins = pe.transpose(wide(3)[0:PS, k * P:(k + 1) * P], hf[:, k, SEQ - PS:SEQ], ident)
                ins.then_inc(pstate_t, 1)
                pe.wait_ge(srow_done, 2)
                pe.wait_ge(exs_new, 1)
                for k in range(KT8):
                    ins = pe.transpose(wide(0)[0:120, k * P:(k + 1) * P], exs_out[:, k, :], ident)
                ins.then_inc(pstate_t, 1)
                for a in range(2):
                    u = U_POOL + a
                    pe.wait_ge(hi_ready, u + 1)
                    pe.wait_ge(lo_ready, u + 1)
                    for d in range(4 * a, 4 * a + 4):
                        gl, m = divmod(d - 4 * a, 2)
                        pe.wait_ge(vlo, KT8 + d // 2 * 2 + 2)
                        for c in range(NC):
                            pe.wait_ge(down_empty, G_POOL + 3 * d + c - 2)
                            products(pe, bank(3 + c)[:, 0:CW], u % 2, 256, slice(m * P, (m + 1) * P),
                                     [(2 * gl + k, d // 2 * 2 + k) for k in range(2)], hhi, hlo,
                                     c).then_inc(down_ready, 1)

            @block.vector
            def _(dve):
                dve.memset(ext[:, :, 0:16], 0.0).then_inc(ext_pad, 1)
                dve.wait_ge(ext_pad, 1)
                dve.wait_ge(srow_done, 2)
                for t in range(DT):
                    ins = dve.tensor_copy(exs[:, :, :, PS + t],
                                          hf[:, :, SEQ:ROWS].rearrange("p k (b t) -> p k b t", t=DT)[:, :, :, t])
                chain(dve, ins, "v", vchain)
                for b in range(NB):
                    ins = dve.tensor_copy(exs_out[:, :, b * PS:(b + 1) * PS], exs[:, :, b, DT:DT + PS])
                ins.then_inc(exs_new, 1)

                def lower(d):
                    dve.wait_ge(pooled_hi, d + 1)
                    dve.tensor_tensor(hlo[:, d, :], pooled[:, d % 2, :], hhi[:, d, :], ALU.subtract).then_inc(vlo, 1)

                for g in range(4):
                    w = 2 << g
                    e = exs[:, 2 * g:2 * g + 2]
                    for k in range(g + 1):
                        n = 1 << k
                        lo = 2 * n - 1
                        prev = e if k == 0 else exa[:, k - 1]
                        for q in range(2):
                            ins = dve.tensor_tensor(exa[:, k, q, :, lo:], prev[:, q, :, lo:], prev[:, q, :, lo - n:PS + DT - n],
                                                    ALU.add)
                        chain(dve, ins, "v", vchain)
                    for d in (2 * g, 2 * g + 1):
                        dve.wait_ge(ext_ready, d + 1)
                        src = ext[:, d % 2]
                        for k in range(g + 1):
                            n = 1 << k
                            lo = 2 * n - 1
                            dst = ext[:, 2 + k % 2]
                            chain(dve, dve.tensor_tensor(dst[:, lo:], src[:, lo:], src[:, lo - n:16 + SEQ - n], ALU.add),
                                  "v", vchain)
                            src = dst
                        chain(dve, dve.tensor_tensor(headcol[:], src[:, 16:32], cst[:, C_INV + 16 * g:C_INV + 16 * g + 16],
                                                     ALU.mult), "v", vchain)
                        dve.tensor_tensor(pooled[:, d % 2, 0:16], headcol[:], hf[:, d, 0:16], ALU.subtract)
                        dve.scalar_tensor_tensor(out=pooled[:, d % 2, 16:SEQ], in0=src[:, 32:], scalar=1.0 / w,
                                                 in1=hf[:, d, 16:SEQ], op0=ALU.mult, op1=ALU.subtract)
                        four = lambda v: v.rearrange("p (b t) -> p b t", t=DT)
                        dve.scalar_tensor_tensor(out=four(pooled[:, d % 2, SEQ:ROWS]), in0=exa[:, g, d % 2, :, PS:],
                                                 scalar=1.0 / w, in1=four(hf[:, d, SEQ:ROWS]), op0=ALU.mult,
                                                 op1=ALU.subtract).then_inc(pooled_done, 1)
                        dve.wait_ge(pooled_done, d + 1)
                        if d >= 1:
                            lower(d - 1)
                    if g >= 2:
                        for d in (2 * g - 4, 2 * g - 3):
                            for c in range(NC):
                                if residual(dve, G_POOL + 3 * d + c, c, d, 1, 16):
                                    residual_end(dve, 72 + d + 1, d)
                lower(KT8 - 1)
                for d in range(4, KT8):
                    for c in range(NC):
                        if residual(dve, G_POOL + 3 * d + c, c, d, 1, 16):
                            residual_end(dve, 72 + d + 1, d)

        norm_block(3, 1, 24, "split")
        mlp_block(1, U_MLP1, G_MLP1, 80)
        norm_block(4, 1, 0, "final")

        with nc.Block() as block:
            @block.tensor
            def _(pe):
                for i in range(TILES + 1):
                    n = P if i < TILES else NS
                    if i >= 2:
                        pe.wait_ge(y_copied, i - 1)
                    for k in range(KT8):
                        ins = pe.transpose(wide(i % 2)[0:n, k * P:(k + 1) * P], hf[:, k, i * P:i * P + n], ident)
                    ins.then_inc(y_t, 1)

            @block.scalar
            def _(act):
                for i in range(TILES + 1):
                    n = P if i < TILES else NS
                    act.wait_ge(y_t, i + 1)
                    if i >= 2:
                        act.wait_ge(yst[i % 2], 16 * (i // 2))
                    act.activation(yrow[0:n, i % 2, :], wide(i % 2)[0:n, :], ACT.Copy).then_inc(y_copied, 1)

            @block.sync
            def _(sp):
                for i in range(TILES + 1):
                    n = P if i < TILES else NS
                    sp.wait_ge(y_copied, i + 1)
                    dst = y_prompt[0, i * P:(i + 1) * P, :] if i < TILES else y_sample.rearrange("b t d -> (b t) d")
                    sp.dma_start(dst, yrow[0:n, i % 2, :]).then_inc(yst[i % 2], 16)
                sp.wait_ge(yst[0], 16 * 5)
                sp.wait_ge(yst[1], 16 * 4)


def u_in_cols(u):
    if u < 2:
        c = QW + KW + u * P
    elif u < 4:
        c = QW + (u - 2) * P
    elif u < 12:
        c = (u - 4) * P
    else:
        c = QW + 2 * KW + (u - 12) * P
    return slice(c, c + P)


def u_in_dst(u, vt, kt, qt, qi, ki2, wi):
    if u < 2:
        return vt[:, u, :], P
    if u < 4:
        return kt[:, u - 2, :], P
    if u < 12:
        return qt[:, u - 4, :], P
    if u < 16:
        return qi[:, u - 12, :], P
    return (ki2[:, :], P) if u == 16 else (wi[:, :], IH)


_INS = ['x_prompt', 'x_sample', 'cache_k', 'cache_v', 'cache_kidx', 'state_pool', 'page_table', 'c_prompt', 'c_sample',
        'norm_mix_g', 'norm_ffn_g', 'w_mod', 'b_mod', 'dsa_w_in', 'dsa_w_o', 'pool_w', 'pool_scale', 'w_up', 'w_down',
        'final_norm_g']
_OUTS = [(1, SEQ, D), (NB, DT, D), (1, 1, SEQ, KV, HD), (1, 1, SEQ, KV, HD), (1, 1, SEQ, ID), (1, 1, PS, D),
         (1, NB, DT, KV, HD), (1, NB, DT, KV, HD), (1, NB, DT, ID), (1, NB, PS, D)]


def kernel(**inputs):
    import numpy as _np
    import concourse.bacc as _bacc
    from concourse import mybir as _mybir
    from concourse.bass_utils import run_bass_kernel_spmd as _run

    nc = _bacc.Bacc("TRN2", target_bir_lowering=False, num_devices=1)
    arrays, args = {}, []
    for name, a in [(n, inputs[n]) for n in _INS] + [("consts", constants())]:
        a = _np.ascontiguousarray(a)
        arrays[f"in_{name}_dram"] = a
        args.append(nc.dram_tensor(f"in_{name}_dram", a.shape, _mybir.dt.from_np(a.dtype), kind="ExternalInput").ap())
    for i, shape in enumerate(_OUTS):
        args.append(nc.dram_tensor(f"out_{i}_dram", shape, F32, kind="ExternalOutput").ap())
    hybrid_step(nc, *args)
    r = _run(nc, [arrays], core_ids=[0])
    return tuple(r.results[0][f"out_{i}_dram"] for i in range(len(_OUTS)))
```
